# Optimizing a Trainium2 kernel written in Bass

```python
import jax, jax.numpy as jnp
from jax import lax
import numpy as np

D_MODEL = 1024
BATCH = 1
SEQ = 256
DEPTH = 1
DEC_BATCH = 8
DEC_SEQ = 1
PAST_LEN = 1024
PAGE_SIZE = 128

R_HEADS = 4
R_DK = 128
R_DV = 256
R_CHUNK = 128
A_HEADS = 8
A_DH = 128
MOBA_BLOCK = 256
MOBA_TOPK = 3
Q_CHUNK = 64
ROPE_THETA = 10000.0
N_GROUPS = 4
EXPERTS_PER_GROUP = 8
N_EXPERTS = N_GROUPS * EXPERTS_PER_GROUP
D_EXPERT = 256
TOP_K_INNER = 2
EPS = 1e-6

R_QK_W = R_HEADS * R_DK
R_V_W = R_HEADS * R_DV
A_W = A_HEADS * A_DH
D_IN = 2 * R_QK_W + 2 * R_V_W + 3 * A_W + 2 * D_MODEL

kernel_name = 'retention_moba_hier_moe_step'

def rmsnorm(x, g):
    xf = x.astype(jnp.float32)
    y = xf * lax.rsqrt(jnp.mean(xf * xf, axis=-1, keepdims=True) + EPS)
    return (y * g.astype(jnp.float32)).astype(x.dtype)

def rope(x, pos):
    half = x.shape[-1] // 2
    inv = ROPE_THETA ** (-jnp.arange(half, dtype=jnp.float32) / half)
    ang = pos.astype(jnp.float32)[:, None] * inv[None, :]
    cos = jnp.cos(ang)[None, :, None, :]
    sin = jnp.sin(ang)[None, :, None, :]
    xf = x.astype(jnp.float32)
    x1, x2 = xf[..., :half], xf[..., half:]
    return jnp.concatenate([x1 * cos - x2 * sin, x2 * cos + x1 * sin], axis=-1).astype(x.dtype)

def project(h, w_in):
    z = jnp.einsum('bld,de->ble', h, w_in)
    sizes = (R_QK_W, R_QK_W, R_V_W, R_V_W, A_W, A_W, A_W, D_MODEL, D_MODEL)
    points = [sum(sizes[:i]) for i in range(1, len(sizes))]
    return jnp.split(z, points, axis=-1)

def retention_log_decay():
    return jnp.log(1.0 - 2.0 ** (-5.0 - jnp.arange(R_HEADS, dtype=jnp.float32)))

def retention_chunk(s, qkv):
    q, k, v = qkv
    L = q.shape[1]
    ld = retention_log_decay()
    i = jnp.arange(L, dtype=jnp.float32)
    diff = i[:, None] - i[None, :]
    dmask = jnp.where(diff >= 0, jnp.exp(ld[:, None, None] * jnp.maximum(diff, 0.0)), 0.0)
    qf, kf, vf = q.astype(jnp.float32), k.astype(jnp.float32), v.astype(jnp.float32)
    scores = jnp.einsum('bihd,bjhd->bhij', qf, kf) * dmask[None]
    inner = jnp.einsum('bhij,bjhe->bihe', scores, vf)
    cross = jnp.einsum('bihd,bhde->bihe', qf, s) * jnp.exp(ld[None, None, :, None] * (i + 1.0)[None, :, None, None])
    k_dec = kf * jnp.exp(ld[None, None, :, None] * (L - 1.0 - i)[None, :, None, None])
    s_new = s * jnp.exp(ld * L)[None, :, None, None] + jnp.einsum('bjhd,bjhe->bhde', k_dec, vf)
    return s_new, inner + cross

def retention(q, k, v, s0, chunk):
    B, L = q.shape[:2]
    nc = L // chunk

    def chunks(t):
        return t.reshape(B, nc, chunk, *t.shape[2:]).swapaxes(0, 1)

    s_fin, o = lax.scan(retention_chunk, s0, (chunks(q), chunks(k), chunks(v)))
    return s_fin, o.swapaxes(0, 1).reshape(B, L, R_HEADS, R_DV)

def retention_output(o, g):
    B, L = o.shape[:2]
    mu = jnp.mean(o, axis=-1, keepdims=True)
    var = jnp.mean(jnp.square(o - mu), axis=-1, keepdims=True)
    y = ((o - mu) * lax.rsqrt(var + EPS)).reshape(B, L, R_V_W)
    return (jax.nn.silu(g.astype(jnp.float32)) * y).astype(g.dtype)

def to_blocks(t):
    B, T, H, dh = t.shape
    nb = -(-T // MOBA_BLOCK)
    t = jnp.pad(t, ((0, 0), (0, nb * MOBA_BLOCK - T), (0, 0), (0, 0)))
    return t.reshape(B, nb, MOBA_BLOCK, H, dh).transpose(0, 3, 1, 2, 4)

def gather_blocks(blocks, idx):
    return jax.vmap(jax.vmap(lambda t, i: t[i]))(blocks, idx)

def moba_attend(q, kb, vb, kmean, q_pos):
    nb = kb.shape[2]
    own = q_pos // MOBA_BLOCK
    qf = q.astype(jnp.float32)
    gate = jnp.einsum('bhqd,bhnd->bhqn', qf, kmean)
    past = jnp.arange(nb)[None, :] < own[:, None]
    gate = jnp.where(past[None, None], gate, -jnp.inf)
    gval, gidx = lax.top_k(gate, min(MOBA_TOPK, nb))
    own_b = jnp.broadcast_to(own[None, None, :, None], gidx.shape[:-1] + (1,)).astype(gidx.dtype)
    idx = jnp.concatenate([gidx, own_b], axis=-1)
    ok = jnp.concatenate([jnp.isfinite(gval), jnp.ones(own_b.shape, dtype=bool)], axis=-1)
    kg = gather_blocks(kb, idx).astype(jnp.float32)
    vg = gather_blocks(vb, idx).astype(jnp.float32)
    key_pos = idx[..., None] * MOBA_BLOCK + jnp.arange(MOBA_BLOCK)
    mask = ok[..., None] & (key_pos <= q_pos[None, None, :, None, None])
    s = jnp.einsum('bhqd,bhqnkd->bhqnk', qf, kg)
    s = jnp.where(mask, s, -jnp.inf)
    sh = s.shape
    p = jax.nn.softmax(s.reshape(sh[:3] + (-1,)), axis=-1).reshape(sh)
    return jnp.einsum('bhqnk,bhqnkd->bhqd', p, vg).astype(q.dtype)

def moba(q, k_all, v_all, q_pos, q_chunk):
    B, L, H, dh = q.shape
    kb = to_blocks(k_all)
    vb = to_blocks(v_all)
    kmean = jnp.mean(kb.astype(jnp.float32), axis=3)
    nq = L // q_chunk
    qc = q.reshape(B, nq, q_chunk, H, dh).transpose(1, 0, 3, 2, 4)
    pc = q_pos.reshape(nq, q_chunk)
    o = lax.map(lambda a: moba_attend(a[0], kb, vb, kmean, a[1]), (qc, pc))
    return o.transpose(1, 0, 3, 2, 4).reshape(B, L, H * dh)

def token_mixers(h, pos, s0, k_past, v_past, r_chunk, q_chunk, w_in, w_ret_o, w_att_o, w_o):
    B, L, _ = h.shape
    rq, rk, rv, rg, aq, ak, av, gr, ga = project(h, w_in)
    rq = rope(rq.reshape(B, L, R_HEADS, R_DK), pos) * (R_DK ** -0.5)
    rk = rope(rk.reshape(B, L, R_HEADS, R_DK), pos)
    rv = rv.reshape(B, L, R_HEADS, R_DV)
    r_state, r_out = retention(rq, rk, rv, s0, r_chunk)
    ret = retention_output(r_out, rg)
    aq = rope(aq.reshape(B, L, A_HEADS, A_DH), pos) * (A_DH ** -0.5)
    ak = rope(ak.reshape(B, L, A_HEADS, A_DH), pos)
    av = av.reshape(B, L, A_HEADS, A_DH)
    if k_past is None:
        k_all, v_all = ak, av
    else:
        k_all = jnp.concatenate([k_past, ak.astype(k_past.dtype)], axis=1)
        v_all = jnp.concatenate([v_past, av.astype(v_past.dtype)], axis=1)
    att = moba(aq, k_all, v_all, pos, q_chunk)
    r = jnp.einsum('ble,ed->bld', ret, w_ret_o)
    a = jnp.einsum('ble,ed->bld', att, w_att_o)
    merged = jax.nn.sigmoid(gr) * r + jax.nn.sigmoid(ga) * a
    return jnp.einsum('bld,de->ble', merged, w_o), ak, av, r_state

def hier_moe(h, w_rg, b_rg, w_re, b_re, w_gate, w_up, w_down):
    glog = jnp.einsum('bld,dg->blg', h, w_rg).astype(jnp.float32) + b_rg.astype(jnp.float32)
    gprob = jax.nn.softmax(glog, axis=-1)
    g_idx = jnp.argmax(glog, axis=-1)
    g_w = jnp.max(gprob, axis=-1)
    elog = jnp.einsum('bld,dge->blge', h, w_re).astype(jnp.float32) + b_re.astype(jnp.float32)
    elog_sel = jnp.einsum('blge,blg->ble', elog, jax.nn.one_hot(g_idx, N_GROUPS, dtype=jnp.float32))
    ev, ei = lax.top_k(elog_sel, TOP_K_INNER)
    ew = jax.nn.softmax(ev, axis=-1)
    flat = g_idx[..., None] * EXPERTS_PER_GROUP + ei
    combine = jnp.sum(jax.nn.one_hot(flat, N_EXPERTS, dtype=jnp.float32) * (g_w[..., None] * ew)[..., None], axis=-2)
    a = jnp.einsum('bld,edf->blef', h, w_gate)
    u = jnp.einsum('bld,edf->blef', h, w_up)
    act = jax.nn.silu(a) * u * combine.astype(h.dtype)[..., None]
    return jnp.einsum('blef,efd->bld', act, w_down)

def setup_inputs(seed: int = 0) -> dict:
    key = jax.random.key(seed)
    ks = jax.random.split(key, 20)
    n_pages = PAST_LEN // PAGE_SIZE
    n_used = DEC_BATCH * n_pages
    n_pool = (n_used * 5 + 3) // 4
    perm = jax.random.permutation(ks[0], n_pool)
    page_table = perm[:n_used].reshape(DEC_BATCH, n_pages).astype(jnp.int32)
    f32 = jnp.float32
    nrm = lambda k, shape, s: jax.random.normal(k, shape, f32) * s
    return {
        'x_prompt': nrm(ks[1], (BATCH, SEQ, D_MODEL), 1.0),
        'x_sample': nrm(ks[2], (DEC_BATCH, DEC_SEQ, D_MODEL), 1.0),
        'cache_k': nrm(ks[3], (DEPTH, n_pool, PAGE_SIZE, A_HEADS, A_DH), 1.0),
        'cache_v': nrm(ks[4], (DEPTH, n_pool, PAGE_SIZE, A_HEADS, A_DH), 1.0),
        'state_ret': nrm(ks[5], (DEPTH, DEC_BATCH, R_HEADS, R_DK, R_DV), 0.1),
        'page_table': page_table,
        'norm_mix': 1.0 + nrm(ks[6], (DEPTH, D_MODEL), 0.02),
        'w_in': nrm(ks[7], (DEPTH, D_MODEL, D_IN), D_MODEL ** -0.5),
        'w_ret_o': nrm(ks[8], (DEPTH, R_V_W, D_MODEL), R_V_W ** -0.5),
        'w_att_o': nrm(ks[9], (DEPTH, A_W, D_MODEL), A_W ** -0.5),
        'w_o': nrm(ks[10], (DEPTH, D_MODEL, D_MODEL), D_MODEL ** -0.5),
        'norm_ffn': 1.0 + nrm(ks[11], (DEPTH, D_MODEL), 0.02),
        'w_router_group': nrm(ks[12], (DEPTH, D_MODEL, N_GROUPS), D_MODEL ** -0.5),
        'b_router_group': nrm(ks[13], (DEPTH, N_GROUPS), 0.01),
        'w_router_expert': nrm(ks[14], (DEPTH, D_MODEL, N_GROUPS, EXPERTS_PER_GROUP), D_MODEL ** -0.5),
        'b_router_expert': nrm(ks[15], (DEPTH, N_GROUPS, EXPERTS_PER_GROUP), 0.01),
        'w_gate': nrm(ks[16], (DEPTH, N_EXPERTS, D_MODEL, D_EXPERT), D_MODEL ** -0.5),
        'w_up': nrm(ks[17], (DEPTH, N_EXPERTS, D_MODEL, D_EXPERT), D_MODEL ** -0.5),
        'w_down': nrm(ks[18], (DEPTH, N_EXPERTS, D_EXPERT, D_MODEL), D_EXPERT ** -0.5),
        'norm_final': 1.0 + nrm(ks[19], (D_MODEL,), 0.02),
    }

def reference(x_prompt, x_sample, cache_k, cache_v, state_ret, page_table, norm_mix, w_in, w_ret_o,
              w_att_o, w_o, norm_ffn, w_router_group, b_router_group, w_router_expert, b_router_expert,
              w_gate, w_up, w_down, norm_final):
    B, S, _ = x_prompt.shape
    DB, DS, _ = x_sample.shape
    past_len = page_table.shape[1] * PAGE_SIZE
    pos_p = jnp.arange(S, dtype=jnp.int32)
    pos_s = past_len + jnp.arange(DS, dtype=jnp.int32)
    yp, ys = x_prompt, x_sample
    kp_l, vp_l, rp_l, ks_l, vs_l, rs_l = [], [], [], [], [], []
    for l in range(DEPTH):
        hp = rmsnorm(yp, norm_mix[l])
        s0 = jnp.zeros((B, R_HEADS, R_DK, R_DV), jnp.float32)
        mp, kp, vp, rp = token_mixers(hp, pos_p, s0, None, None, R_CHUNK, Q_CHUNK,
                                      w_in[l], w_ret_o[l], w_att_o[l], w_o[l])
        yp = yp + mp
        yp = yp + hier_moe(rmsnorm(yp, norm_ffn[l]), w_router_group[l], b_router_group[l],
                           w_router_expert[l], b_router_expert[l], w_gate[l], w_up[l], w_down[l])
        k_past = cache_k[l][page_table].reshape(DB, past_len, A_HEADS, A_DH)
        v_past = cache_v[l][page_table].reshape(DB, past_len, A_HEADS, A_DH)
        hs = rmsnorm(ys, norm_mix[l])
        ms, kn, vn, rn = token_mixers(hs, pos_s, state_ret[l].astype(jnp.float32), k_past, v_past, DS, DS,
                                      w_in[l], w_ret_o[l], w_att_o[l], w_o[l])
        ys = ys + ms
        ys = ys + hier_moe(rmsnorm(ys, norm_ffn[l]), w_router_group[l], b_router_group[l],
                           w_router_expert[l], b_router_expert[l], w_gate[l], w_up[l], w_down[l])
        kp_l.append(kp)
        vp_l.append(vp)
        rp_l.append(rp.astype(x_prompt.dtype))
        ks_l.append(kn.astype(cache_k.dtype))
        vs_l.append(vn.astype(cache_v.dtype))
        rs_l.append(rn.astype(state_ret.dtype))
    y_prompt = rmsnorm(yp, norm_final)
    y_sample = rmsnorm(ys, norm_final)
    k_prompt = jnp.stack(kp_l)
    v_prompt = jnp.stack(vp_l)
    ret_prompt = jnp.stack(rp_l)
    k_sample = jnp.stack(ks_l)
    v_sample = jnp.stack(vs_l)
    ret_sample = jnp.stack(rs_l)
    return (y_prompt, y_sample, k_prompt, v_prompt, ret_prompt, k_sample, v_sample, ret_sample)


_drawn_inputs = setup_inputs


def setup_inputs(seed=0):
    import zlib

    import numpy as np

    out = dict(_drawn_inputs(seed))
    spreads = {}
    factors = {'b_router_group': 8.0, 'b_router_expert': 5.99, 'norm_final': 2.826}
    for name, (base, spread) in spreads.items():
        noise = np.random.default_rng([zlib.crc32(name.encode()), seed]).standard_normal(out[name].shape)
        drawn = base * np.exp(spread * noise) if base else spread * noise
        out[name] = __import__('jax').numpy.asarray(drawn.astype(out[name].dtype))
    for name, factor in factors.items():
        out[name] = (out[name] * factor).astype(out[name].dtype)
    return out
```

```python
from contextlib import ExitStack

import numpy as np

import concourse.bass as bass
from concourse import mybir
from concourse.alu_op_type import AluOpType as ALU

ACT = mybir.ActivationFunctionType
AX = mybir.AxisListType
F32 = mybir.dt.float32
I32 = mybir.dt.int32

P = 128
DM = 1024
KT = DM // P
S = 256
NB = 8
T = S + NB
RH, RDV = 4, 256
AH, DH = 8, 128
PAST = 1024
NPG = PAST // P
NPOOL = 80
G, EPG = 4, 8
NE = G * EPG
DE = 256
FB = DE // P
CAP = 64
XT = (2 * T) // (CAP + 1)
NT = NE + XT
BIG = 1.0e30
EPS = 1e-6
TOPK = 3

ROWS = (P, P, NB)

_WIDTHS = [("ident", P), ("ones", P), ("upper", P), ("causal", 3 * P), ("rmask", RH * P), ("rdec", RH * P),
           ("kdec", RH), ("rope", 3 * 4 * 64), ("edge", NT + 1), ("slot", CAP), ("first", NE), ("gidx", G),
           ("eidx", EPG), ("tok", 3), ("tile", XT), ("diag", NB * NB), ("own", AH),
           ("before", 16), ("after", 16), ("spread", NB * AH)]
COL, _at = {}, 0
for _n, _w in _WIDTHS:
    COL[_n] = (_at, _at + _w)
    _at += _w
CW = _at


def shape_constants():
    c = np.zeros((P, CW), np.float32)

    def put(name, value, rows=P):
        a, b = COL[name]
        c[:rows, a:b] = np.asarray(value, np.float32).reshape(-1, b - a)

    i = np.arange(P, dtype=np.float32)
    ld = np.log(np.float32(1) - np.float32(2) ** (-5 - np.arange(RH, dtype=np.float32))).astype(np.float32)
    put("ident", np.eye(P))
    put("ones", np.ones((P, P)))
    put("upper", i[:, None] < i[None, :])
    causal = np.where(i[None, :] <= i[:, None], 0.0, -BIG)
    put("causal", np.concatenate([causal, np.zeros((P, P)), causal], 1))
    diff = i[None, :] - i[:, None]
    put("rmask", np.stack([np.where(diff >= 0, np.exp(x * np.maximum(diff, 0)), 0) for x in ld], 1))
    put("rdec", np.tile(np.exp(ld[:, None] * (i + 1)).reshape(1, -1), (P, 1)))
    put("kdec", np.exp(ld[None, :] * (P - 1 - i)[:, None]))
    inv = (np.float32(10000.0) ** (-np.arange(64, dtype=np.float32) / np.float32(64))).astype(np.float32)
    rope = np.zeros((P, 3, 4, 64), np.float32)
    for t in range(3):
        pos = i + P * t if t < 2 else np.full(P, PAST, np.float32)
        ang = (pos[:, None].astype(np.float32) * inv[None, :]).astype(np.float32)
        rope[:, t, 0], rope[:, t, 1] = np.cos(ang), np.sin(ang)
        rope[:, t, 2], rope[:, t, 3] = np.cos(ang) * DH ** -0.5, np.sin(ang) * DH ** -0.5
    put("rope", rope.reshape(P, -1))
    put("edge", np.tile(CAP * np.arange(NT + 1), (P, 1)))
    put("slot", np.tile(np.arange(CAP), (P, 1)))
    put("first", np.tile(CAP * np.arange(NE), (P, 1)))
    put("gidx", np.tile(np.arange(G), (P, 1)))
    put("eidx", np.tile(np.arange(EPG), (P, 1)))
    put("tok", i[:, None] + P * np.arange(3)[None, :])
    put("tile", np.tile(np.arange(XT), (P, 1)))
    put("diag", np.tile(np.eye(NB).reshape(1, -1), (P, 1)))
    put("own", np.tile(np.eye(AH), (NB, 1)), NB * AH)
    n, m = np.meshgrid(np.arange(4), np.arange(4), indexing="ij")
    put("before", np.tile((m < n).reshape(1, -1), (P, 1)))
    put("after", np.tile((m > n).reshape(1, -1), (P, 1)))
    put("spread", np.repeat(np.eye(NB), AH, 1), NB)
    return c


LD = [float(np.log(1.0 - 2.0 ** (-5.0 - h))) for h in range(RH)]

ZR = 1024
RING = 6
UC = 256
N_IN = 8192 // UC
N_ATT, N_RET, N_GATE = 12, 12, 8
N_O = DM // UC
N_V = NB * NPG // 2
U_RETO = N_IN
U_V = U_RETO + N_O
U_ATTO = U_V + N_V
U_WO = U_ATTO + N_O
U_MOE = U_WO + N_O
KRING = 3
N_FIRST = 6


def in_column(n):
    if n < N_ATT:
        return 3072 + UC * n
    if n < N_ATT + N_RET:
        return UC * (n - N_ATT)
    return UC * n


def unit_signals(n):
    return 32 if U_V <= n < U_ATTO else 16


def slot_value(n):
    return sum(unit_signals(k) for k in range(n % RING, n + 1, RING))


def pages_until(n):
    return 0 if n < N_FIRST else (NB * NPG * (n - N_FIRST + 1)) // (N_IN - N_FIRST)


def build(nc, x_prompt, x_sample, cache_k, cache_v, state_ret, page_table, norm_mix, w_in, w_ret_o, w_att_o,
          w_o, norm_ffn, w_rg, b_rg, w_re, b_re, w_gate, w_up, w_down, norm_final, consts,
          y_prompt, y_sample, k_prompt, v_prompt, ret_prompt, k_sample, v_sample, ret_sample):
    ctx = ExitStack()
    with ctx:
        def sb(name, shape, dt=F32):
            return ctx.enter_context(nc.sbuf_tensor(name, shape, dt))

        def pb(name, shape):
            return ctx.enter_context(nc.psum_tensor(name, shape, F32))

        def sem(name):
            return ctx.enter_context(nc.semaphore(name))

        h2_rows = nc.dram_tensor("h2_rows", [T, DM], F32, kind="Internal").ap()
        y_rows = nc.dram_tensor("y_rows", [NT * CAP, DM], F32, kind="Internal").ap()

        ring = [sb(f"ring{i}", [P, 2048]) for i in range(RING)]
        kpage = [sb(f"kpage{i}", [P, DM]) for i in range(KRING)]
        cst = sb("cst", [P, CW])
        gain = sb("gain", [P, DM])
        xs = sb("xs", [P, 3, DM])
        hT = sb("hT", [P, KT, T])
        zatt = sb("zatt", [P, 2, 3072])
        zret = sb("zret", [P, 2, 3072])
        zdec = sb("zdec", [NB, 4096])
        attT = sb("attT", [P, AH, T])
        retT = sb("retT", [P, AH, T])
        zt = [sb(f"zt{i}", [P, T]) for i in range(2)]
        qb = [sb(f"qb{i}", [P, DM]) for i in range(2)]
        junkx = qb[1]
        scores = sb("scores", [P, NPG, NB * AH])
        vnT = sb("vnT", [P, NB * AH])
        sn8 = sb("sn8", [NB, AH])
        rtmp = sb("rtmp", [P, 2, 2, P])
        rtmd = sb("rtmd", [NB, 2, 2, P])
        qkT = sb("qkT", [P, 4 * P])
        sm = sb("sm", [P, 3 * P])
        pT = sb("pT", [P, 3 * P])
        st = sb("st", [P, 16])
        kdd = sb("kdd", [P, 2, RH, P])
        qdT = sb("qdT", [P, P])
        s1 = sb("s1", [P, RDV])
        sfin = sb("sfin", [P, RDV])
        rsig = sb("rsig", [P, 2, RDV])
        qkd = sb("qkd", [P, 2, RH * NB])
        qmask = sb("qmask", [P, RH, NB, NB])
        ptab = sb("ptab", [1, NB * NPG], I32)
        wr = sb("wr", [P, KT, G + NE])
        brt = sb("brt", [P, G + NE])
        hnat = zret[:, :, :].rearrange("p a b -> p (a b)")[:, 0:3 * DM].rearrange("p (t d) -> p t d", t=3)
        zflat = zatt[:, :, :].rearrange("p a b -> p (a b)")
        sigT = zflat[:, 0:16 * T].rearrange("p (g t) -> p g t", g=16)
        mT = hT
        heads = lambda ap: ap.rearrange("p (h e) -> p h e", h=RH)
        stt = [heads(zflat[:, 16 * T:16 * T + DM]), heads(xs[:, 0, :])]
        snw = [heads(xs[:, 1, :]), heads(xs[:, 2, :])]
        zr = zret[:, :, :].rearrange("p a b -> p (a b)")
        sc64 = zr[0:64, 0:PAST]
        pw = zr[:, 1984:1984 + NPG * 512 + 64]
        pw_own = [pw[:, 512 * p:512 * p + 576].rearrange("p (b c) -> p b c", c=72)[:, :, 0:AH] for p in range(NPG)]
        dvn = zr[:, 1600:1664]
        dcol = zr[0:64, 1700:1764]
        sm64 = zr[0:64, 1800:1900]
        mtmp = [qb[0][:, T * i:T * (i + 1)] for i in range(2)]
        h2T = attT
        rt = zr[:, 2560:6144]
        xg = [zflat[0:CAP, DM * i:DM * (i + 1)] for i in range(2)]
        ysb = [zflat[0:CAP, 2 * DM + DM * i:3 * DM + DM * i] for i in range(2)]
        xgT = [retT[:, :, :].rearrange("p a b -> p (a b)")[:, 512 * i:512 * (i + 1)] for i in range(2)]
        acT = [retT[:, :, :].rearrange("p a b -> p (a b)")[:, 1024 + 128 * i:1152 + 128 * i] for i in range(2)]
        hid = [retT[:, :, :].rearrange("p a b -> p (a b)")[0:CAP, 1280 + DE * i:1280 + DE * (i + 1)] for i in range(2)]

        h2n = zflat[:, 0:3 * DM].rearrange("p (t d) -> p t d", t=3)
        fbuf = [zflat[:, 4 * DM + DM * i:5 * DM + DM * i] for i in range(2)]
        qrow, krow = zdec[:, 0:DM], zdec[:, DM:2 * DM]
        rgd = qrow
        rod = qb[1][0:NB, :]
        gst = sb("gst", [P, 12])
        gy = sb("gy", [P, RDV])
        taddr_i = sb("taddr_i", [P, 6], I32)
        tidx_i = sb("tidx_i", [CAP, NT], I32)
        tcol = sb("tcol", [CAP, 2], I32)
        texp_i = sb("texp_i", [1, XT + 1], I32)
        wk = sb("wk", [P, 3, 2])
        r_at = [0]

        def small(rows, *dims):
            w = int(np.prod(dims))
            ap = rt[0:rows, r_at[0]:r_at[0] + w]
            r_at[0] += w
            if len(dims) == 2:
                ap = ap.rearrange("p (a b) -> p a b", a=dims[0])
            if len(dims) == 3:
                ap = ap.rearrange("p (a b c) -> p a b c", a=dims[0], b=dims[1])
            return ap

        lg, tex1, el, el2, tw = small(P, 3, G + NE), small(P, 3, G + 1), small(P, 3, EPG), small(P, 3, EPG), small(P, 3, EPG)
        ew4 = small(P, 3, G, EPG)
        ghot, hot1, hot2 = small(P, 3, G), small(P, 3, EPG), small(P, 3, EPG)
        gmx, m1, m2, imin, gsum, wsum = (small(P, 3) for _ in range(6))
        oh1, oh2, oh, posn, slotn = (small(P, 3, NE) for _ in range(5))
        over, addr = small(P, NE), small(P, 3, 2)
        xcnt, xtmp, xcnt_b = small(NE, 1), small(NE, 1), small(NE, P)
        ge, rem, onA, onB = small(P, NT + 1), small(P, 1), small(P, 6, CAP), small(P, 6, NT)
        xcum, xt2, xexp, xall = small(1, NE), small(1, NE), small(1, XT + 1), small(1, 1)
        assert r_at[0] <= 3584

        zps = [pb(f"zps{i}", [P, 512]) for i in range(2)]
        nps = [pb(f"nps{i}", [P, 512]) for i in range(2)]
        bps = pb("bps", [P, 1024])
        mps = pb("mps", [P, 1024])

        def cc(name, rows=P):
            a, b = COL[name]
            return cst[0:rows, a:b]

        ident, ones, upper = cc("ident"), cc("ones"), cc("upper")

        (s_x, s_gain, s_const, s_tab, s_router_in) = map(sem, ("x_in", "gain_in", "const_in", "page_table_in", "router_in"))
        slot_in = [sem(f"slot_in{i}") for i in range(RING)]
        k_in = [sem(f"k_in{i}") for i in range(KRING)]
        v_used, e_G, page_done, dve, acts = map(sem, ("v_used", "e_G", "page_done", "dve_chain", "act_chain"))
        h_ready, hT_ps, hT_done = map(sem, ("h_ready", "hT_ps", "hT_done"))
        z_ready, zt_done, n_ready, n_done = map(sem, ("z_ready", "zt_done", "n_ready", "n_done"))
        z_free = [sem(f"z_free{i}") for i in range(2)]
        rope_done, pchain = map(sem, ("rope_done", "pool_chain"))
        qb_ps, qb_done = map(sem, ("qb_ps", "qb_done"))
        out_done = sem("out_done")
        a_T, a_Tc, a_S, a_P, a_PT, a_PTc, a_O, a_Oc, a_mx, a_ex, a_sc = map(sem, (
            "a_T", "a_Tc", "a_S", "a_P", "a_PT", "a_PTc", "a_O", "a_Oc", "a_mx", "a_ex", "a_sc"))
        r_T, r_Tc, r_B, r_Bc, r_Bs, r_qd, r_C, r_fin, r_N, r_X, r_Xc, r_sig, r_st = map(sem, (
            "r_T", "r_Tc", "r_B", "r_Bc", "r_Bs", "r_qd", "r_C", "r_fin", "r_N", "r_X", "r_Xc", "r_sig", "r_st"))
        d_T, d_Tc, d_V, d_S, d_O, d_mul, d_sig, d_N, d_X, d_Xc, d_qm = map(sem, (
            "d_T", "d_Tc", "d_V", "d_S", "d_O", "d_mul", "d_sig", "d_N", "d_X", "d_Xc", "d_qm"))
        st_in = [sem(f"st_in{i}") for i in range(2)]
        st_out = [sem(f"st_out{i}") for i in range(2)]
        kd_done = sem("kd_done")
        f_S, f_mx, f_ex, f_P, f_PT, f_PTc, f_att, f_new, f_nT, f_mm = map(sem, (
            "f_S", "f_mx", "f_ex", "f_P", "f_PT", "f_PTc", "f_att", "f_new", "f_nT", "f_mm"))
        m_done, h2_out, pw_zero, f_vo, f_own = map(sem, ("m_done", "h2_out", "pw_zero", "f_vo", "f_own"))
        h2_ready, h2T_ps, h2T_done, t_log, t_oh, t_pos, t_x, t_exp, t_tabs, t_idx, t_lhs, t_e2 = map(sem, (
            "h2_ready", "h2T_ps", "h2T_done", "t_log", "t_oh", "t_pos", "t_x", "t_exp", "t_tabs", "t_idx", "t_lhs", "t_e2"))
        x_in2 = [sem(f"xg_in{i}") for i in range(2)]
        e_T, e_Tc, e_GU, e_sg, e_ac, e_H, e_Hc, e_D, e_Dc = map(sem, (
            "e_T", "e_Tc", "e_GU", "e_sg", "e_ac", "e_H", "e_Hc", "e_D", "e_Dc"))
        y_out = [sem(f"y_out{i}") for i in range(2)]
        y_fill = sem("y_fill")
        o_w, pe_turn, pool_turn = map(sem, ("o_w", "pe_turn", "pool_turn"))
        o_x = sem("o_x")
        fg_in = [sem(f"fg_in{i}") for i in range(2)]
        fy = sem("fy")
        fgain = sem("fgain")


        block = ctx.enter_context(nc.Block())

        @block.sync
        def _(sp):
            sp.dma_start(ptab[:, :], page_table.rearrange("b n -> (b n)").rearrange("(o n) -> o n", o=1)).then_inc(s_tab, 16)

            def slot_free(n):
                old = n - RING
                if old < 0:
                    return
                if old < U_RETO:
                    sp.wait_ge(z_ready, 2 * (old + 1))
                elif old < U_V:
                    sp.wait_ge(z_ready, 2 * (old - U_RETO + 1) + 64)
                elif old < U_ATTO:
                    sp.wait_ge(v_used, old - U_V + 1)
                else:
                    sp.wait_ge(z_ready, 2 * (old - U_ATTO + 1) + 72)

            def unit(n, out, src):
                slot_free(n)
                sp.dma_start(out, src).then_inc(slot_in[n % RING], 16)

            def col_unit(n, w, c, inner):
                src = w.rearrange("(p k) c -> p k c", k=KT) if inner else w.rearrange("(k p) c -> p k c", p=P)
                unit(n, ring[n % RING][:, :].rearrange("p (k c) -> p k c", k=KT), src[:, :, c:c + UC])

            tab_waited = False
            pages = 0
            for n in range(N_IN):
                col_unit(n, w_in[0], in_column(n), True)
                if n >= 3 and not tab_waited:
                    sp.wait_ge(s_tab, 16)
                    tab_waited = True
                while pages < pages_until(n):
                    p = pages
                    if p >= KRING:
                        sp.wait_ge(page_done, p - KRING + 1)
                    pid = sp.value_load(ptab[0:1, p:p + 1], min_val=0, max_val=NPOOL - 1)
                    sp.dma_start(kpage[p % KRING][:, :],
                                 cache_k[0, bass.ds(pid, 1)].rearrange("o s h d -> (o s) (h d)")).then_inc(k_in[p % KRING], 16)
                    pages += 1
            for j in range(N_O):
                col_unit(U_RETO + j, w_ret_o[0], UC * j, False)
            for j in range(N_V):
                n = U_V + j
                slot_free(n)
                for k in range(2):
                    pid = sp.value_load(ptab[0:1, 2 * j + k:2 * j + k + 1], min_val=0, max_val=NPOOL - 1)
                    sp.dma_start(ring[n % RING][:, DM * k:DM * (k + 1)],
                                 cache_v[0, bass.ds(pid, 1)].rearrange("o s h d -> (o s) (h d)")).then_inc(slot_in[n % RING], 16)
            for j in range(N_O):
                col_unit(U_ATTO + j, w_att_o[0], UC * j, False)
            for j in range(N_O):
                col_unit(U_WO + j, w_o[0], UC * j, False)

            def expert_unit(k, e):
                s = (U_MOE + k) % RING
                if k % 3 == 2:
                    sp.dma_start(ring[s][:, :].rearrange("p (f n) -> p f n", f=FB),
                                 w_down[0, bass.ds(e, 1)].rearrange("o (f p) n -> p (o f) n", p=P)).then_inc(slot_in[s], 16)
                else:
                    w = w_gate if k % 3 == 0 else w_up
                    sp.dma_start(ring[s][:, :],
                                 w[0, bass.ds(e, 1)].rearrange("o (p k) f -> p (o k f)", k=KT)).then_inc(slot_in[s], 16)

            for k in range(6):
                slot_free(U_MOE + k)
                expert_unit(k, k // 3)
            with sp.Fori(1, NE // 2) as i:
                for k in range(6):
                    sp.wait_ge((e_G, e_GU, e_D)[k % 3], i * 2 + (k // 3 - 1))
                    expert_unit(k, i * 2 + k // 3)
            sp.wait_ge(t_exp, 1)
            extra = sp.value_load(texp_i[0:1, XT:XT + 1], min_val=0, max_val=XT)
            with sp.Fori(0, XT // 2) as j:
                for a in range(2):
                    with sp.If(extra > j * 2 + a):
                        ex = sp.value_load(texp_i[0:1, bass.ds(j * 2 + a, 1)], min_val=0, max_val=NE - 1)
                        for k in range(3):
                            sp.wait_ge((e_G, e_GU, e_D)[k], j * 2 + (NE + a - 1))
                            expert_unit(3 * a + k, ex)

        @block.gpsimd
        def _(pool):
            link_n = [0]

            def link(ins):
                link_n[0] += 1
                ins.then_inc(pchain, 1)
                pool.wait_ge(pchain, link_n[0])

            def rope(z, zd, c, q, cd=0):
                for x, tmp, rows, t0, nt in ((z, rtmp, P, 0, 2), (zd, rtmd, NB, 2, 1)):
                    v = (x[:, 0:2, c:c + 256] if nt == 2 else x[0:NB, c + cd:c + cd + 256].unsqueeze(1))
                    a0, _ = COL["rope"]
                    tab = cst[0:rows, a0 + 256 * t0:a0 + 256 * (t0 + nt)].rearrange("p (t f d) -> p t f d", t=nt, f=4)
                    cos, sin = (tab[:, :, f + (2 if q else 0), :] for f in (0, 1))
                    for h in range(2):
                        x1, x2 = v[:, :, 128 * h:128 * h + 64], v[:, :, 128 * h + 64:128 * h + 128]
                        ta, tb = tmp[0:rows, 0:nt, h, 0:64], tmp[0:rows, 0:nt, h, 64:128]
                        pool.tensor_tensor(ta, x2, sin, ALU.mult)
                        link(pool.tensor_tensor(tb, x1, sin, ALU.mult))
                        pool.tensor_tensor(x1, x1, cos, ALU.mult)
                        link(pool.tensor_tensor(x2, x2, cos, ALU.mult))
                        pool.tensor_tensor(x1, x1, ta, ALU.subtract)
                        link(pool.tensor_tensor(x2, x2, tb, ALU.add))

            for k in range(XT * CAP // S):
                pool.dma_start(y_rows[NE * CAP + S * k:NE * CAP + S * (k + 1), :], x_prompt[0]).then_inc(y_fill, 16)
            pool.wait_ge(s_const, 16)
            for n in range(8):
                pool.wait_ge(n_done, 4 * (n + 1))
                rope(zatt, zdec, 256 * n, n < 4)
                pool.sem_inc(rope_done, 1)
            for t in range(2):
                pool.dma_start(k_prompt[0, 0].rearrange("s h d -> s (h d)")[P * t:P * (t + 1), :],
                               zatt[:, t, 1024:2048]).then_inc(out_done, 16)
            pool.dma_start(k_sample[0, :, 0].rearrange("b h d -> b (h d)"), zdec[0:NB, 1024:2048]).then_inc(out_done, 16)
            pool.wait_ge(n_done, 4 * N_ATT)
            for t in range(2):
                pool.dma_start(v_prompt[0, 0].rearrange("s h d -> s (h d)")[P * t:P * (t + 1), :],
                               zatt[:, t, 2048:3072]).then_inc(out_done, 16)
            pool.dma_start(v_sample[0, :, 0].rearrange("b h d -> b (h d)"), zdec[0:NB, 2048:3072]).then_inc(out_done, 16)
            for n in range(4):
                pool.wait_ge(n_done, 4 * (N_ATT + n + 1))
                rope(zret, zdec, 256 * n, n < 2, ZR)
                pool.sem_inc(rope_done, 1)
            a, b_ = COL["kdec"]
            for t in range(2):
                pool.tensor_tensor(kdd[:, t, :, :], zret[:, t, 512:1024].rearrange("p (h d) -> p h d", h=RH),
                                   cst[:, a:b_].unsqueeze(2).to_broadcast([P, RH, P]), ALU.mult).then_inc(kd_done, 1)
            pool.wait_ge(a_O, AH)
            for b in range(2):
                pool.dma_start(stt[b], state_ret[0, b].rearrange("h k v -> k h v")).then_inc(st_in[b], 16)
            for b in range(NB):
                pool.wait_ge(d_S, RH * (b + 1))
                pool.dma_start(ret_sample[0, b].rearrange("h k v -> k h v"), snw[b % 2]).then_inc(st_out[b % 2], 16)
                if b + 2 < NB:
                    pool.dma_start(stt[b % 2], state_ret[0, b + 2].rearrange("h k v -> k h v")).then_inc(st_in[b % 2], 16)

            pool.wait_ge(r_X, RH)
            pool.memset(pw, 0.0).then_inc(pw_zero, 1)

            for t, r in enumerate(ROWS):
                pool.wait_ge(h2_ready, t + 1)
                pool.dma_start(h2_rows[P * t:P * t + r, :], h2n[0:r, t, :]).then_inc(h2_out, 16)
            pool.wait_ge(h2_out, 48)
            pool.wait_ge(t_idx, 1)

            def gather(par):
                pool.indirect_dma_start(out=xg[par], out_offset=None, in_=h2_rows,
                                        in_offset=bass.IndirectOffsetOnAxis(ap=tcol[:, par:par + 1], axis=0),
                                        bounds_check=T - 1, oob_is_err=False).then_inc(x_in2[par], 16)

            for par in range(2):
                link(pool.tensor_copy(tcol[:, par:par + 1], tidx_i[:, par:par + 1]))
                gather(par)
            base = link_n[0]
            with pool.Fori(0, (NE - 2) // 2) as i:
                for par in range(2):
                    pool.wait_ge(e_T, i * 2 + (par + 1))
                    pool.wait_ge(x_in2[par], i * 16 + 16)
                    pool.tensor_copy(tcol[:, par:par + 1], tidx_i[:, bass.ds(i * 2 + (2 + par), 1)]).then_inc(pchain, 1)
                    pool.wait_ge(pchain, i * 2 + (base + par + 1))
                    pool.sem_inc(pool_turn, 1)
                    gather(par)
            base += NE - 2
            extra = pool.value_load(texp_i[0:1, XT:XT + 1], min_val=0, max_val=XT)
            with pool.Fori(0, XT) as j:
                with pool.If(extra > j):
                    pool.wait_ge(e_T, j + NE)
                    pool.tensor_copy(tcol[:, 0:1], tidx_i[:, bass.ds(j + NE, 1)]).then_inc(pchain, 1)
                    pool.wait_ge(pchain, j + (base + 1))
                    pool.sem_inc(pool_turn, 1)
                    gather(0)
                    pool.wait_ge(y_out[0], j * 16 + 16 * (NE // 2 + 1))
                    pool.sem_inc(pool_turn, 1)
            pool.wait_ge(y_fill, 16 * (XT * CAP // S))
            pool.wait_ge(y_out[0], 16 * (NE // 2))
            pool.wait_ge(y_out[1], 16 * (NE // 2))
            for q in range(6):
                t, k = q // 2, q % 2
                r = ROWS[t]
                if q >= 2:
                    pool.wait_ge(fy, t)
                pool.indirect_dma_start(out=fbuf[k][0:r, :], out_offset=None, in_=y_rows,
                                        in_offset=bass.IndirectOffsetOnAxis(ap=taddr_i[0:r, 2 * t + k:2 * t + k + 1], axis=0),
                                        bounds_check=NT * CAP - 1, oob_is_err=False).then_inc(fg_in[k], 16)
            pool.wait_ge(out_done, 16 * 6)
            pool.wait_ge(st_out[0], 64)
            pool.wait_ge(st_out[1], 64)

        @block.scalar
        def _(act):
            act.dma_start(cst[:, :], consts).then_inc(s_const, 16)

            def load_x():
                for t in range(2):
                    act.dma_start(xs[:, t, :], x_prompt[0, P * t:P * (t + 1), :]).then_inc(s_x, 16)
                act.dma_start(xs[0:NB, 2, :], x_sample.rearrange("b s d -> (b s) d")).then_inc(s_x, 16)

            load_x()
            act.dma_start(gain[:, :], norm_mix.partition_broadcast(P).rearrange("p o d -> p (o d)")).then_inc(s_gain, 16)
            act.dma_start(wr[:, :, 0:G], w_rg[0].rearrange("(p k) g -> p k g", k=KT)).then_inc(s_router_in, 16)
            act.dma_start(wr[:, :, G:G + NE], w_re[0].rearrange("(p k) g e -> p k (g e)", k=KT)).then_inc(s_router_in, 16)
            act.dma_start(brt[:, 0:G], b_rg.partition_broadcast(P).rearrange("p o d -> p (o d)")).then_inc(s_router_in, 16)
            act.dma_start(brt[:, G:G + NE], b_re.partition_broadcast(P).rearrange("p o g e -> p (o g e)")).then_inc(s_router_in, 16)

            chain = [0]

            def link(ins):
                chain[0] += 1
                ins.then_inc(acts, 1)
                act.wait_ge(acts, chain[0])

            def copy(out, in_):
                return act.activation(out, in_, ACT.Copy)

            act.wait_ge(h_ready, 3)
            act.dma_start(gain[:, :], norm_ffn.partition_broadcast(P).rearrange("p o d -> p (o d)")).then_inc(s_gain, 16)
            for k in range(KT):
                act.wait_ge(hT_ps, k + 1)
                copy(hT[:, k, :], zps[k % 2][:, 0:T]).then_inc(hT_done, 1)

            def qbcast(b):
                act.wait_ge(qb_ps, b + 1)
                if b >= 2:
                    act.wait_ge(page_done, NPG * (b - 1))
                copy(qb[b % 2][:, :], bps[:, :]).then_inc(qb_done, 1)

            def rows_of(q):
                act.wait_ge(n_ready, q + 1)
                z, c = (zatt, P * q) if q < 24 else (zret, P * (q - 24))
                ps = nps[q % 2][:, 0:384].rearrange("p (t d) -> p t d", t=3)
                if q == 24:
                    act.wait_ge(f_nT, 1)
                    act.wait_ge(out_done, 96)
                copy(z[:, :, c:c + P], ps[:, 0:2, :]).then_inc(n_done, 1)
                c += 0 if q < 24 else ZR
                copy(zdec[0:NB, c:c + P], ps[0:NB, 2, :]).then_inc(n_done, 1)

            def block_rows(m):
                act.wait_ge(z_ready, m + 1)
                if m >= 2:
                    act.wait_ge(n_ready, m - 1)
                if 16 <= m < 24:
                    h = m - 16
                    copy(vnT[:, h:64:8], zps[m % 2][:, S:T]).then_inc(f_new, 1)
                copy(zt[m % 2][:, :], zps[m % 2][:, 0:T]).then_inc(zt_done, 1)
                if m >= 1:
                    rows_of(m - 1)

            for n in range(N_ATT + N_RET):
                for b in range(NB):
                    if n >= N_FIRST and pages_until(n - 1) <= NPG * b < pages_until(n):
                        qbcast(b)
                for fb in range(2):
                    block_rows(2 * n + fb)
                    if n >= N_ATT:
                        s = 2 * (n - N_ATT) + fb
                        if s % 3 == 0 and s > 0:
                            act.wait_ge(a_O, s // 3)
                            copy(attT[:, s // 3 - 1, 0:S], mps[:, 0:S]).then_inc(a_Oc, 1)
                        h, k = s // 3, s % 3
                        if k == 0:
                            act.wait_ge(a_T, h + 1)
                            copy(qkT[:, :], mps[:, 0:512]).then_inc(a_Tc, 1)
                        if k == 1:
                            act.wait_ge(a_mx, h + 1)
                            for t, (lo, hi) in enumerate(((0, 128), (128, 384))):
                                act.activation(sm[:, lo:hi], sm[:, lo:hi], ACT.Exp, bias=st[:, t:t + 1],
                                               accum_out=st[:, 2 + t:3 + t]).then_inc(a_ex, 1)
                        if k == 2:
                            act.wait_ge(a_PT, h + 1)
                            copy(pT[:, :], mps[:, 512:896]).then_inc(a_PTc, 1)
            rows_of(47)
            act.wait_ge(a_O, AH)
            copy(attT[:, AH - 1, 0:S], mps[:, 0:S]).then_inc(a_Oc, 1)

            act.wait_ge(n_done, 96)
            act.wait_ge(d_T, 1)
            copy(qkd[:, :, :].rearrange("p a b -> p (a b)"), mps[:, 0:64]).then_inc(d_Tc, 1)
            for n in range(N_GATE):
                for b in range(NB):
                    if pages_until(23 + n) <= NPG * b < pages_until(24 + n):
                        qbcast(b)
                for fb in range(2):
                    m = 48 + 2 * n + fb
                    act.wait_ge(z_ready, m + 1)
                    act.activation(sigT[:, 2 * n + fb, :], zps[m % 2][:, 0:T], ACT.Sigmoid).then_inc(z_free[m % 2], 1)
                    s = 2 * n + fb
                    r, k = s // 4, s % 4
                    if k == 0:
                        act.wait_ge(r_T, r + 1)
                        if r >= 1:
                            act.wait_ge(r_N, r)
                        copy(qkT[:, :], nps[0][:, :]).then_inc(r_Tc, 1)
                        act.activation(rsig[:, :, :], zret[:, :, 2048 + RDV * r:2048 + RDV * (r + 1)], ACT.Sigmoid).then_inc(r_sig, 1)
                    if k == 1:
                        act.wait_ge(r_B, r + 1)
                        act.wait_ge(r_Bc, r + 1)
                        copy(s1[:, :], nps[1][:, 256:512]).then_inc(r_Bs, 1)
                    if k == 3:
                        act.wait_ge(r_fin, r + 1)
                        act.dma_start(ret_prompt[0, 0, r], sfin[:, :]).then_inc(r_st, 16)
                        act.wait_ge(r_X, r + 1)
                        copy(retT[:, 2 * r:2 * r + 2, 0:S], nps[1][:, :].rearrange("p (a b) -> p a b", a=2)).then_inc(r_Xc, 1)
                b = n
                act.wait_ge(st_in[b % 2], 16 * (b // 2 + 1))
                for h in range(RH):
                    act.activation(stt[b % 2][:, h, :], stt[b % 2][:, h, :], ACT.Copy,
                                   scale=float(np.exp(LD[h]))).then_inc(d_mul, 1)
            act.wait_ge(qb_ps, NB)
            act.activation(rgd, zdec[0:NB, ZR + 2048:ZR + 3072], ACT.Sigmoid).then_inc(d_sig, 1)
            act.wait_ge(d_X, 1)
            copy(retT[:, :, S:T], nps[0][:, 0:64].rearrange("p (k b) -> p k b", k=8)).then_inc(d_Xc, 1)

            act.wait_ge(f_mx, 1)
            act.activation(sc64, sc64, ACT.Exp, bias=sm64[:, 2:3], accum_out=sm64[:, 3:4]).then_inc(f_ex, 1)
            act.activation(sm64[:, 4:5], sm64[:, 1:2], ACT.Exp, bias=sm64[:, 2:3]).then_inc(f_ex, 1)
            act.wait_ge(f_PT, 1)
            act.wait_ge(pw_zero, 1)
            for p in range(NPG):
                copy(pw_own[p], bps[:, 64 * p:64 * (p + 1)].rearrange("p (b h) -> p b h", b=NB)).then_inc(f_PTc, 1)

            act.wait_ge(y_fill, 16 * (XT * CAP // S))
            act.wait_ge(st_out[0], 16 * NB // 2)
            act.wait_ge(st_out[1], 16 * NB // 2)
            act.wait_ge(d_O, NB)
            load_x()
            act.wait_ge(v_used, N_V)
            for c in range(2):
                copy(sc64[:, 512 * c:512 * (c + 1)], nps[c][0:64, :]).then_inc(f_vo, 1)
            for k in range(8):
                m, q = 80 + k, 48 + k
                act.wait_ge(z_ready, m + 1)
                act.wait_ge(n_ready, q - 1)
                copy(zt[m % 2][:, :], zps[m % 2][:, 0:T]).then_inc(zt_done, 1)

            for k in range(KT):
                act.wait_ge(h2T_ps, k + 1)
                copy(h2T[:, k, :], zps[k % 2][:, 0:T]).then_inc(h2T_done, 1)
            act.wait_ge(t_lhs, 1)
            act.activation(tex1, tex1, ACT.Exp).then_inc(t_e2, 1)

            def x_copy(par, n):
                act.wait_ge(e_T, n)
                copy(xgT[par], zps[par][:, :]).then_inc(e_Tc, 1)

            def silu(par, n):
                act.wait_ge(e_GU, n)
                act.activation(hid[par], nps[par][0:CAP, 0:DE], ACT.Silu).then_inc(e_sg, 1)

            def h_copy(par, n, used):
                act.wait_ge(e_H, n)
                if used is not None:
                    act.wait_ge(e_D, used)
                copy(acT[par], zps[par][:, 0:FB * CAP]).then_inc(e_Hc, 1)

            def store(par, n, row):
                act.wait_ge(e_Dc, n)
                act.dma_start(y_rows[row, :], ysb[par]).then_inc(y_out[par], 16)

            x_copy(0, 1)
            silu(0, 1)
            x_copy(1, 2)
            h_copy(0, 1, None)
            silu(1, 2)
            x_copy(0, 3)
            h_copy(1, 2, None)
            store(0, 1, slice(0, CAP))
            with act.Fori(0, (NE - 2) // 2) as i:
                for a in range(2):
                    silu(a, i * 2 + (a + 3))
                    if a == 0:
                        x_copy(1, i * 2 + 4)
                    else:
                        with act.If(i < (NE - 2) // 2 - 1):
                            x_copy(0, i * 2 + 5)
                    h_copy(a, i * 2 + (a + 3), i * 2 + (a + 1))
                    store(1 - a, i * 2 + (a + 2), bass.ds(i * (2 * CAP) + CAP * (a + 1), CAP))
            store(1, NE, slice(CAP * (NE - 1), CAP * NE))
            extra = act.value_load(texp_i[0:1, XT:XT + 1], min_val=0, max_val=XT)
            with act.Fori(0, XT) as j:
                with act.If(extra > j):
                    x_copy(0, j + (NE + 1))
                    silu(0, j + (NE + 1))
                    h_copy(0, j + (NE + 1), j + NE)
                    store(0, j + (NE + 1), bass.ds(j * CAP + NE * CAP, CAP))
            act.dma_start(gain[:, :], norm_final.rearrange("(o d) -> o d", o=1).partition_broadcast(P)
                          .rearrange("p o d -> p (o d)")).then_inc(fgain, 16)
            for t in range(3):
                act.wait_ge(o_x, t + 1)
                out = y_prompt[0, P * t:P * (t + 1), :] if t < 2 else y_sample.rearrange("b s d -> (b s) d")
                act.dma_start(out, xs[0:ROWS[t], t, :]).then_inc(o_w, 16)
            act.wait_ge(o_w, 48)
            act.wait_ge(r_st, 16 * RH)

        @block.tensor
        def _(pe):
            pe.wait_ge(s_const, 16)

            def tr(out, in_, rows):
                return pe.transpose(out, in_, ident[0:rows, 0:rows])

            def all_tiles(ps, src, k):
                for t, r in enumerate(ROWS):
                    mm = tr(ps[:, P * t:P * t + r], src[0:r, t, k:DM:KT], r)
                return mm

            pe.wait_ge(h_ready, 3)
            for k in range(KT):
                if k >= 2:
                    pe.wait_ge(hT_done, k - 1)
                all_tiles(zps[k % 2], hnat, k).then_inc(hT_ps, 1)
            pe.wait_ge(hT_done, KT)

            def features(n, fb, m, rhs):
                if fb == 0:
                    pe.wait_ge(slot_in[n % RING], slot_value(n))
                w = ring[n % RING][:, :].rearrange("p (k c) -> p k c", k=KT)
                for k in range(KT):
                    mm = pe.matmul(zps[m % 2][:, 0:T], w[:, k, P * fb:P * (fb + 1)], rhs[:, k, :],
                                   start=(k == 0), stop=(k == KT - 1))
                mm.then_inc(z_ready, 1)

            def rows_of(q, zi):
                pe.wait_ge(zt_done, q + 1)
                if q >= 2:
                    pe.wait_ge(n_done, 2 * (q - 1))
                for t, r in enumerate(ROWS):
                    mm = tr(nps[q % 2][0:r, P * t:P * (t + 1)], zt[zi][:, P * t:P * t + r], P)
                mm.then_inc(n_ready, 1)

            def qbcast(b):
                if b == 0:
                    pe.wait_ge(rope_done, 4)
                if b >= 1:
                    pe.wait_ge(qb_done, b)
                for c in range(2):
                    mm = pe.matmul(bps[:, 512 * c:512 * (c + 1)], ident[0:NB, b:b + 1].to_broadcast([NB, P]),
                                   qrow[:, 512 * c:512 * (c + 1)], start=True, stop=True)
                mm.then_inc(qb_ps, 1)

            def a_stage(h, k):
                if k == 3:
                    pe.wait_ge(a_PTc, h + 1)
                    if h == 0:
                        pe.wait_ge(n_done, 4 * N_ATT)
                    v0, v1 = (zatt[:, t, 2048 + P * h:2048 + P * (h + 1)] for t in range(2))
                    pe.matmul(mps[:, 0:128], v0, pT[:, 0:128], start=True, stop=True)
                    pe.matmul(mps[:, 128:256], v0, pT[:, 128:256], start=True, stop=False)
                    pe.matmul(mps[:, 128:256], v1, pT[:, 256:384], start=False, stop=True).then_inc(a_O, 1)
                if k == 0:
                    pe.wait_ge(rope_done, 8)
                    if h >= 1:
                        pe.wait_ge(a_Oc, h)
                    for a in range(2):
                        for t in range(2):
                            mm = tr(mps[:, 256 * a + P * t:256 * a + P * (t + 1)],
                                    zatt[:, t, 1024 * a + P * h:1024 * a + P * (h + 1)], P)
                    mm.then_inc(a_T, 1)
                if k == 1:
                    pe.wait_ge(a_Tc, h + 1)
                    if h >= 1:
                        pe.wait_ge(a_PTc, h)
                    pe.matmul(mps[:, 512:640], qkT[:, 0:128], qkT[:, 256:384], start=True, stop=True)
                    pe.matmul(mps[:, 640:896], qkT[:, 128:256], qkT[:, 256:512], start=True, stop=True).then_inc(a_S, 1)
                if k == 2:
                    pe.wait_ge(a_P, h + 1)
                    for a in range(3):
                        mm = tr(mps[:, 512 + P * a:512 + P * (a + 1)], sm[:, P * a:P * (a + 1)], P)
                    mm.then_inc(a_PT, 1)

            for n in range(N_ATT + N_RET):
                for b in range(NB):
                    if n >= N_FIRST and pages_until(n - 1) <= NPG * b < pages_until(n):
                        qbcast(b)
                for fb in range(2):
                    m = 2 * n + fb
                    if m >= 2:
                        pe.wait_ge(zt_done, m - 1)
                    features(n, fb, m, hT)
                    if m >= 1:
                        rows_of(m - 1, (m - 1) % 2)
                    if n >= N_ATT:
                        s = 2 * (n - N_ATT) + fb
                        if s % 3 == 0 and s > 0:
                            a_stage(s // 3 - 1, 3)
                        a_stage(s // 3, s % 3)
            rows_of(47, 1)
            a_stage(AH - 1, 3)

            pe.wait_ge(rope_done, 12)
            pe.wait_ge(a_Oc, AH)
            for a in range(2):
                for h in range(RH):
                    c = 32 * a + 8 * h
                    mm = tr(mps[:, c:c + NB], zdec[0:NB, ZR + 512 * a + P * h:ZR + 512 * a + P * (h + 1)], NB)
            mm.then_inc(d_T, 1)

            def d_out(b):
                if b == 0:
                    pe.wait_ge(d_Tc, 1)
                    pe.wait_ge(d_qm, 1)
                pe.wait_ge(d_S, RH * (b + 1))
                for h in range(RH):
                    mm = pe.matmul(mps[0:NB, RDV * h:RDV * (h + 1)], qmask[:, h, b, :], snw[b % 2][:, h, :],
                                   start=(b == 0 and h % 2 == 0), stop=(b == NB - 1),
                                   skip_group_check=True)
                mm.then_inc(d_O, 1)

            def r_stage(r, k):
                v0, v1 = (zret[:, t, 1024 + RDV * r:1024 + RDV * (r + 1)] for t in range(2))
                if k == 0:
                    if r == 0:
                        pe.wait_ge(n_done, 96)
                    else:
                        pe.wait_ge(r_N, r)
                    for a in range(2):
                        for t in range(2):
                            mm = tr(nps[0][:, 256 * a + P * t:256 * a + P * (t + 1)],
                                    zret[:, t, 512 * a + P * r:512 * a + P * (r + 1)], P)
                    mm.then_inc(r_T, 1)
                if k == 1:
                    pe.wait_ge(r_Tc, r + 1)
                    if r >= 1:
                        pe.wait_ge(r_Xc, r)
                    for t in range(2):
                        pe.matmul(nps[1][:, P * t:P * (t + 1)], qkT[:, 256 + P * t:256 + P * (t + 1)],
                                  qkT[:, P * t:P * (t + 1)], start=True, stop=True)
                    pe.wait_ge(kd_done, 2)
                    pe.matmul(nps[1][:, 256:512], kdd[:, 0, r, :], v0, start=True, stop=True).then_inc(r_B, 1)
                if k == 2:
                    pe.wait_ge(r_Bc, r + 1)
                    pe.wait_ge(r_Bs, r + 1)
                    pe.wait_ge(r_qd, r + 1)
                    pe.matmul(nps[0][:, 0:256], sm[:, 0:128], v0, start=True, stop=True)
                    pe.matmul(nps[0][:, 256:512], sm[:, 128:256], v1, start=True, stop=False)
                    pe.matmul(nps[0][:, 256:512], qdT[:, :], s1[:, :], start=False, stop=True)
                    pe.matmul(nps[1][:, 0:256], kdd[:, 1, r, :], v1, start=True, stop=True).then_inc(r_C, 1)
                if k == 3:
                    pe.wait_ge(r_N, r + 1)
                    pe.wait_ge(r_fin, r + 1)
                    for j in range(2):
                        for t in range(2):
                            mm = tr(nps[1][:, 256 * j + P * t:256 * j + P * (t + 1)],
                                    zret[:, t, 2048 + RDV * r + P * j:2048 + RDV * r + P * (j + 1)], P)
                    mm.then_inc(r_X, 1)

            for n in range(N_GATE):
                for b in range(NB):
                    if pages_until(23 + n) <= NPG * b < pages_until(24 + n):
                        if n >= 1:
                            pe.wait_ge(d_S, RH * n)
                        qbcast(b)
                for fb in range(2):
                    m = 48 + 2 * n + fb
                    if m < 50:
                        pe.wait_ge(zt_done, m - 1)
                    else:
                        pe.wait_ge(z_free[m % 2], (m - 48) // 2)
                    features(24 + n, fb, m, hT)
                    s = 2 * n + fb
                    r_stage(s // 4, s % 4)
                b = n
                if b >= 1:
                    pe.wait_ge(d_S, RH * b)
                pe.wait_ge(qb_done, min(NB, -(-pages_until(24 + n) // NPG)))
                for c in range(2):
                    mm = pe.matmul(bps[:, 512 * c:512 * (c + 1)], ident[0:NB, b:b + 1].to_broadcast([NB, P]),
                                   zdec[0:NB, ZR + 1024 + 512 * c:ZR + 1024 + 512 * (c + 1)], start=True, stop=True)
                mm.then_inc(d_V, 1)
                if b >= 1:
                    d_out(b - 1)
            d_out(NB - 1)
            pe.wait_ge(page_done, NB * NPG)
            pe.wait_ge(d_S, RH * NB)
            for p in range(NPG):
                tr(bps[0:64, P * p:P * (p + 1)], scores[:, p, :], P)
            pe.wait_ge(f_nT, 1)
            pe.wait_ge(z_free[0], 8)
            pe.matmul(zps[0][0:64, 0:AH], cc("spread", NB), sn8[:, :], start=True, stop=True).then_inc(f_S, 1)
            pe.wait_ge(d_N, 1)
            pe.wait_ge(r_N, RH)
            for k in range(8):
                mm = tr(nps[0][:, NB * k:NB * (k + 1)], rod[:, P * k:P * (k + 1)], NB)
            mm.then_inc(d_X, 1)
            pe.wait_ge(d_Xc, 1)
            pe.wait_ge(r_Xc, RH)

            for n in range(N_O):
                for fb in range(2):
                    m = 64 + 2 * n + fb
                    if m == 64:
                        pe.wait_ge(f_mm, 1)
                    pe.wait_ge(z_free[m % 2], (m - 48) // 2)
                    features(U_RETO + n, fb, m, retT)
            pe.wait_ge(f_P, 1)
            for p in range(NPG):
                tr(bps[:, 64 * p:64 * (p + 1)], sc64[:, P * p:P * (p + 1)], 64)
            pe.matmul(bps[:, 512:576], ones[0:64, :], dcol, start=True, stop=True).then_inc(f_PT, 1)
            pe.wait_ge(f_PTc, NPG)
            for j in range(N_V):
                n = U_V + j
                b = j // 4
                pe.wait_ge(slot_in[n % RING], slot_value(n))
                for k in range(2):
                    p = 2 * (j % 4) + k
                    for c in range(2):
                        mm = pe.matmul(nps[c][0:64, :], pw[:, 512 * p + 64 * b:512 * p + 64 * (b + 1)],
                                       ring[n % RING][:, DM * k + 512 * c:DM * k + 512 * (c + 1)],
                                       start=(j == 0 and k == 0), stop=(j == N_V - 1 and k == 1))
                mm.then_inc(v_used, 1)
            pe.wait_ge(f_vo, 2)
            for h in range(AH):
                mm = pe.matmul(mps[:, NB * h:NB * (h + 1)], sc64[:, P * h:P * (h + 1)], ident[0:64, h:64:AH],
                               start=True, stop=True)
            mm.then_inc(f_own, 1)
            pe.wait_ge(f_att, 1)
            for n in range(N_O):
                for fb in range(2):
                    m = 72 + 2 * n + fb
                    pe.wait_ge(z_free[m % 2], (m - 48) // 2)
                    features(U_ATTO + n, fb, m, attT)
            pe.wait_ge(m_done, 8)
            for n in range(N_O):
                for fb in range(2):
                    m = 80 + 2 * n + fb
                    k = 2 * n + fb
                    if k < 2:
                        pe.wait_ge(z_free[m % 2], (m - 48) // 2)
                    else:
                        pe.wait_ge(zt_done, 48 + k - 1)
                    features(U_WO + n, fb, m, mT)
                    if k >= 1:
                        rows_of(48 + k - 1, (m - 1) % 2)
            rows_of(55, 1)
            pe.wait_ge(h2_ready, 3)
            pe.wait_ge(zt_done, 56)
            for k in range(KT):
                if k >= 2:
                    pe.wait_ge(h2T_done, k - 1)
                all_tiles(zps[k % 2], h2n, k).then_inc(h2T_ps, 1)
            pe.wait_ge(h2T_done, KT)
            pe.wait_ge(s_router_in, 64)
            for t, r in enumerate(ROWS):
                for k in range(KT):
                    mm = pe.matmul(bps[0:r, 64 * t:64 * t + G + NE], h2T[:, k, P * t:P * t + r], wr[:, k, :],
                                   start=(k == 0), stop=(k == KT - 1))
            mm.then_inc(t_log, 1)
            pe.wait_ge(t_oh, 1)
            for t, r in enumerate(ROWS):
                for u in range(t + 1):
                    ru = ROWS[u]
                    lhs = ones[0:ru, 0:r] if u < t else upper[0:ru, 0:r]
                    pe.matmul(mps[0:r, NE * t:NE * (t + 1)], lhs, oh[0:ru, u, :], start=(u == 0), stop=(u == t))
            for t, r in enumerate(ROWS):
                mm = pe.matmul(mps[0:NE, 256:257], oh[0:r, t, :], ones[0:r, 0:1], start=(t == 0), stop=(t == 2))
            mm.then_inc(t_pos, 1)
            pe.wait_ge(t_x, 1)
            pe.matmul(mps[:, 512:512 + NE], xcnt_b, upper[0:NE, 0:NE], start=True, stop=True)
            pe.matmul(mps[:, 768:769], xcnt_b, ones[0:NE, 0:1], start=True, stop=True).then_inc(t_tabs, 1)
            pe.wait_ge(t_tabs, 1)
            pe.wait_ge(t_lhs, 2)
            for q in range(6):
                t, k = q // 2, q % 2
                r = ROWS[t]
                mm = pe.matmul(nps[0][0:CAP, 0:NT], onA[0:r, q, :], onB[0:r, q, :], start=(q == 0), stop=(q == 5))
            mm.then_inc(t_tabs, 1)

            sl = [(U_MOE + k) % RING for k in range(6)]
            landed = [slot_value(U_MOE + k) for k in range(6)]

            def x_tr(par, x_value, h_used):
                if h_used is not None:
                    pe.wait_ge(e_Hc, h_used)
                pe.wait_ge(x_in2[par], x_value)
                pe.sem_inc(pe_turn, 1)
                for k in range(KT):
                    mm = pe.transpose(zps[par][:, CAP * k:CAP * (k + 1)], xg[par][:, k:DM:KT], ident[0:CAP, 0:CAP])
                mm.then_inc(e_T, 1)

            def gate_up(par, half, n, more):
                pe.wait_ge(e_Tc, n)
                for a in range(2):
                    s = 3 * half + a
                    pe.wait_ge(slot_in[sl[s]], more + landed[s])
                    w = ring[sl[s]][:, :].rearrange("p (k f) -> p k f", k=KT)
                    for k in range(KT):
                        mm = pe.matmul(nps[par][0:CAP, DE * a:DE * (a + 1)], xgT[par][:, CAP * k:CAP * (k + 1)], w[:, k, :],
                                       start=(k == 0), stop=(k == KT - 1))
                    mm.then_inc((e_G, e_GU)[a], 1)

            def h_tr(par, n):
                pe.wait_ge(e_ac, n)
                pe.sem_inc(pe_turn, 1)
                for f in range(FB):
                    mm = pe.transpose(zps[par][:, CAP * f:CAP * (f + 1)], hid[par][:, P * f:P * (f + 1)], ident[0:CAP, 0:CAP])
                mm.then_inc(e_H, 1)

            def down(par, half, n, more, y_used):
                y = (bps, mps)[par]
                s = 3 * half + 2
                pe.wait_ge(e_Hc, n)
                if y_used is not None:
                    pe.wait_ge(e_Dc, y_used)
                pe.wait_ge(slot_in[sl[s]], more + landed[s])
                w = ring[sl[s]][:, :].rearrange("p (f n) -> p f n", f=FB)
                for c in range(2):
                    for f in range(FB):
                        mm = pe.matmul(y[0:CAP, 512 * c:512 * (c + 1)], acT[par][:, CAP * f:CAP * (f + 1)],
                                       w[:, f, 512 * c:512 * (c + 1)], start=(f == 0), stop=(f == FB - 1))
                mm.then_inc(e_D, 1)

            pe.wait_ge(t_idx, 1)
            x_tr(0, 16, None)
            gate_up(0, 0, 1, 0)
            x_tr(1, 16, None)
            h_tr(0, 1)
            gate_up(1, 1, 2, 0)
            x_tr(0, 32, 1)
            down(0, 0, 1, 0, None)
            h_tr(1, 2)
            with pe.Fori(0, (NE - 2) // 2) as i:
                for a in range(2):
                    gate_up(a, a, i * 2 + (a + 3), i * 16 + 16)
                    if a == 0:
                        x_tr(1, i * 16 + 32, i * 2 + 2)
                    else:
                        with pe.If(i < (NE - 2) // 2 - 1):
                            x_tr(0, i * 16 + 48, i * 2 + 3)
                    down(1 - a, 1 - a, i * 2 + (a + 2), i * 16 + 16 * a, i * 2 + 1)
                    h_tr(a, i * 2 + (a + 3))
            down(1, 1, NE, 16 * (NE // 2 - 1), NE - 2)
            extra = pe.value_load(texp_i[0:1, XT:XT + 1], min_val=0, max_val=XT)
            with pe.Fori(0, XT // 2) as j:
                for a in range(2):
                    with pe.If(extra > j * 2 + a):
                        x_tr(0, j * 32 + 16 * (a + NE // 2 + 1), j * 2 + (a + NE))
                        gate_up(0, a, j * 2 + (a + NE + 1), j * 16 + 16 * (NE // 2))
                        h_tr(0, j * 2 + (a + NE + 1))
                        down(0, a, j * 2 + (a + NE + 1), j * 16 + 16 * (NE // 2), j * 2 + (a + NE))

        @block.vector
        def _(v):
            chain = [0]

            def link(ins):
                chain[0] += 1
                ins.then_inc(dve, 1)
                v.wait_ge(dve, chain[0])

            def rsqrt(y, x, t):
                link(v.tensor_scalar(t.bitcast(I32), x.bitcast(I32), 1, None, ALU.logical_shift_right))
                link(v.tensor_scalar(y.bitcast(I32), t.bitcast(I32), -1.0, float(0x5F3759DF), ALU.mult, ALU.add))
                for _ in range(4):
                    link(v.scalar_tensor_tensor(out=t, in0=y, scalar=x, in1=y, op0=ALU.mult, op1=ALU.mult))
                    link(v.tensor_scalar(t, t, -0.5, 1.5, ALU.mult, ALU.add))
                    link(v.tensor_tensor(y, y, t, ALU.mult))

            def norm_rows(src, gain, out, t, ready):
                r = ROWS[t]
                link(v.tensor_tensor_reduce(junkx[0:r, :], src[0:r, t, :], src[0:r, t, :], 1.0, 0.0, ALU.mult, ALU.add,
                                            st[0:r, 8:9]))
                link(v.tensor_scalar(st[0:r, 9:10], st[0:r, 8:9], 1.0 / DM, EPS, ALU.mult, ALU.add))
                rsqrt(st[0:r, 10:11], st[0:r, 9:10], st[0:r, 11:12])
                link(v.scalar_tensor_tensor(out=out[0:r, t, :], in0=src[0:r, t, :], scalar=st[0:r, 10:11],
                                            in1=gain[0:r, :], op0=ALU.mult, op1=ALU.mult))
                if ready is not None:
                    v.sem_inc(ready, 1)

            v.wait_ge(s_x, 48)
            v.wait_ge(s_gain, 16)
            v.wait_ge(s_const, 16)
            for t in range(3):
                norm_rows(xs, gain, hnat, t, h_ready)

            pages = 0

            def page(p):
                b, pg = p // NPG, p % NPG
                v.wait_ge(k_in[p % KRING], 16 * (p // KRING + 1))
                if pg == 0:
                    v.wait_ge(qb_done, b + 1)
                for h in range(AH):
                    kh = kpage[p % KRING][:, P * h:P * (h + 1)]
                    ins = v.tensor_tensor_reduce(kh, kh, qb[b % 2][:, P * h:P * (h + 1)], 1.0, 0.0, ALU.mult, ALU.add,
                                                 scores[:, pg, AH * b + h:AH * b + h + 1])
                ins.then_inc(page_done, 1)

            def a_soft(h):
                v.wait_ge(a_S, h + 1)
                if h >= 1:
                    v.wait_ge(a_PT, h)
                link(v.tensor_tensor(sm[:, :], mps[:, 512:896], cc("causal"), ALU.add))
                v.tensor_reduce(st[:, 0:1], sm[:, 0:128], AX.X, ALU.max, negate=True)
                link(v.tensor_reduce(st[:, 1:2], sm[:, 128:384], AX.X, ALU.max, negate=True))
                v.sem_inc(a_mx, 1)
                v.wait_ge(a_ex, 2 * (h + 1))
                link(v.reciprocal(st[:, 4:6], st[:, 2:4]))
                v.tensor_scalar(sm[:, 0:128], sm[:, 0:128], st[:, 4:5], None, ALU.mult)
                link(v.tensor_scalar(sm[:, 128:384], sm[:, 128:384], st[:, 5:6], None, ALU.mult))
                v.sem_inc(a_P, 1)

            for n in range(N_ATT + N_RET):
                if n == N_ATT:
                    v.wait_ge(rope_done, 8)
                    for h in range(AH):
                        kh = krow[0:NB, P * h:P * (h + 1)]
                        ins = v.tensor_tensor_reduce(zdec[:, 3 * DM + P * h:3 * DM + P * (h + 1)], qrow[0:NB, P * h:P * (h + 1)], kh,
                                                     1.0, 0.0, ALU.mult, ALU.add, sn8[:, h:h + 1])
                    ins.then_inc(f_nT, 1)
                while pages < pages_until(n):
                    page(pages)
                    pages += 1
                if n >= N_ATT:
                    for fb in range(2):
                        s = 2 * (n - N_ATT) + fb
                        if s % 3 == 1:
                            a_soft(s // 3)

            def r_soft(r, k):
                if k == 1:
                    v.wait_ge(r_Tc, r + 1)
                    a, _ = COL["rdec"]
                    if r >= 1:
                        v.wait_ge(r_C, r)
                    v.tensor_tensor(qdT[:, :], qkT[:, 128:256], cst[:, a + P * r:a + P * (r + 1)], ALU.mult).then_inc(r_qd, 1)
                    v.wait_ge(r_B, r + 1)
                    a, _ = COL["rmask"]
                    for t in range(2):
                        ins = v.tensor_tensor(sm[:, P * t:P * (t + 1)], nps[1][:, P * t:P * (t + 1)],
                                              cst[:, a + P * r:a + P * (r + 1)], ALU.mult)
                    ins.then_inc(r_Bc, 1)
                if k == 2:
                    v.wait_ge(r_C, r + 1)
                    v.wait_ge(r_Bs, r + 1)
                    if r >= 1:
                        v.wait_ge(r_st, 16 * r)
                    link(v.scalar_tensor_tensor(out=sfin[:, :], in0=s1[:, :], scalar=float(np.exp(LD[r] * P)),
                                                in1=nps[1][:, 0:256], op0=ALU.mult, op1=ALU.add))
                    v.sem_inc(r_fin, 1)
                    v.wait_ge(r_sig, r + 1)
                    for t in range(2):
                        group_norm(nps[0][:, 256 * t:256 * (t + 1)], rsig[:, t, :],
                                   zret[:, t, 2048 + RDV * r:2048 + RDV * (r + 1)], P)
                    v.sem_inc(r_N, 1)

            def group_norm(o, sig, gate, rows):
                link(v.bn_stats(gst[0:rows, 0:6], o))
                link(v.bn_aggr(gst[0:rows, 6:8], gst[0:rows, 0:6]))
                link(v.tensor_scalar(gst[0:rows, 9:10], gst[0:rows, 7:8], EPS, None, ALU.add))
                rsqrt(gst[0:rows, 8:9], gst[0:rows, 9:10], gst[0:rows, 10:11])
                v.tensor_scalar(gy[0:rows, :], o, gst[0:rows, 6:7], gst[0:rows, 8:9], ALU.subtract, ALU.mult)
                link(v.tensor_tensor(gate, gate, sig, ALU.mult))
                link(v.tensor_tensor(gate, gate, gy[0:rows, :], ALU.mult))

            v.wait_ge(d_Tc, 1)
            for h in range(RH):
                ins = v.tensor_tensor(qmask[:, h, :, :], qkd[:, 0, NB * h:NB * (h + 1)].unsqueeze(1).to_broadcast([P, NB, NB]),
                                      cc("diag").rearrange("p (a b) -> p a b", a=NB), ALU.mult)
            ins.then_inc(d_qm, 1)
            for n in range(N_GATE):
                while pages < pages_until(24 + n):
                    page(pages)
                    pages += 1
                for fb in range(2):
                    s = 2 * n + fb
                    if s % 4 in (1, 2):
                        r_soft(s // 4, s % 4)
                b = n
                v.wait_ge(d_V, b + 1)
                v.wait_ge(d_mul, RH * (b + 1))
                if b >= 2:
                    v.wait_ge(st_out[b % 2], 16 * (b // 2))
                    v.wait_ge(d_O, b - 1)
                for h in range(RH):
                    v.scalar_tensor_tensor(out=snw[b % 2][:, h, :], in0=bps[:, RDV * h:RDV * (h + 1)],
                                           scalar=qkd[:, 1, NB * h + b:NB * h + b + 1], in1=stt[b % 2][:, h, :],
                                           op0=ALU.mult, op1=ALU.add).then_inc(d_S, 1)
            v.wait_ge(d_O, NB)
            v.wait_ge(d_sig, 1)
            for h in range(RH):
                link(v.tensor_copy(rod[:, RDV * h:RDV * (h + 1)], zdec[0:NB, ZR + 2048 + RDV * h:ZR + 2048 + RDV * (h + 1)]))
                group_norm(mps[0:NB, RDV * h:RDV * (h + 1)], rgd[:, RDV * h:RDV * (h + 1)],
                           rod[:, RDV * h:RDV * (h + 1)], NB)
            v.sem_inc(d_N, 1)

            v.wait_ge(f_S, 1)
            v.wait_ge(r_X, RH)
            link(v.tensor_tensor(sm64[:, 8:16], zps[0][0:64, 0:AH], cc("own", 64), ALU.mult))
            link(v.tensor_reduce(sm64[:, 1:2], sm64[:, 8:16], AX.X, ALU.add))
            v.sem_inc(f_mm, 1)
            link(v.tensor_copy(sc64, bps[0:64, :]))
            g4 = sm64[:, 16:20]
            link(v.tensor_reduce(g4, sc64.rearrange("p (n k) -> p n k", n=4), AX.X, ALU.add))
            gm, gn = g4.unsqueeze(1).to_broadcast([64, 4, 4]), g4.unsqueeze(2).to_broadcast([64, 4, 4])
            w1, w2 = sm64[:, 20:36], sm64[:, 36:52]
            v.tensor_tensor(w1.rearrange("p (n m) -> p n m", n=4), gm, gn, ALU.is_ge)
            link(v.tensor_tensor(w2.rearrange("p (n m) -> p n m", n=4), gm, gn, ALU.is_gt))
            v.tensor_tensor(w1, w1, cc("before", 64), ALU.mult)
            link(v.tensor_tensor(w2, w2, cc("after", 64), ALU.mult))
            link(v.tensor_tensor(w1, w1, w2, ALU.add))
            cnt = sm64[:, 52:56]
            link(v.tensor_reduce(cnt, w1.rearrange("p (n m) -> p n m", n=4), AX.X, ALU.add))
            link(v.tensor_scalar(cnt, cnt, TOPK - 0.5, -BIG, ALU.is_gt, ALU.mult))
            link(v.tensor_tensor(sc64.rearrange("p (n k) -> p n k", n=4), sc64.rearrange("p (n k) -> p n k", n=4),
                                 cnt.unsqueeze(2).to_broadcast([64, 4, 256]), ALU.add))
            link(v.tensor_reduce(sm64[:, 0:1], sc64, AX.X, ALU.max))
            link(v.tensor_tensor(sm64[:, 0:1], sm64[:, 0:1], sm64[:, 1:2], ALU.max))
            link(v.tensor_scalar(sm64[:, 2:3], sm64[:, 0:1], -1.0, None, ALU.mult))
            v.sem_inc(f_mx, 1)
            v.wait_ge(f_ex, 2)
            link(v.tensor_tensor(sm64[:, 5:6], sm64[:, 3:4], sm64[:, 4:5], ALU.add))
            link(v.reciprocal(sm64[:, 6:7], sm64[:, 5:6]))
            link(v.tensor_tensor(sm64[:, 7:8], sm64[:, 4:5], sm64[:, 6:7], ALU.mult))
            link(v.tensor_scalar(dcol, cc("ident", 64)[:, 0:64], sm64[:, 7:8], None, ALU.mult))
            link(v.tensor_scalar(sc64, sc64, sm64[:, 6:7], None, ALU.mult))
            v.sem_inc(f_P, 1)

            for k in range(8):
                m = 64 + k
                v.wait_ge(z_ready, m + 1)
                v.tensor_tensor(mT[:, k, :], zps[m % 2][:, 0:T], sigT[:, k, :], ALU.mult).then_inc(z_free[m % 2], 1)
            v.wait_ge(f_PT, 1)
            v.wait_ge(f_new, 8)
            link(v.tensor_tensor(dvn, bps[:, 512:576], vnT[:, :], ALU.mult))
            v.wait_ge(f_own, 1)
            link(v.tensor_tensor(attT[:, :, S:T], mps[:, 0:64].rearrange("p (h b) -> p h b", h=AH),
                                 dvn.rearrange("p (b h) -> p h b", b=NB), ALU.add))
            v.sem_inc(f_att, 1)
            for k in range(8):
                m = 72 + k
                v.wait_ge(z_ready, m + 1)
                v.tensor_tensor(mtmp[k % 2], zps[m % 2][:, 0:T], sigT[:, 8 + k, :], ALU.mult).then_inc(z_free[m % 2], 1)
                v.wait_ge(z_free[m % 2], (m - 48) // 2 + 1)
                v.tensor_tensor(mT[:, k, :], mT[:, k, :], mtmp[k % 2], ALU.add).then_inc(m_done, 1)
            v.wait_ge(s_x, 96)
            for k in range(8):
                q = 48 + k
                v.wait_ge(n_ready, q + 1)
                ps = nps[q % 2][:, 0:384].rearrange("p (t d) -> p t d", t=3)
                v.tensor_tensor(xs[:, 0:2, P * k:P * (k + 1)], xs[:, 0:2, P * k:P * (k + 1)], ps[:, 0:2, :],
                                ALU.add).then_inc(n_done, 1)
                v.tensor_tensor(xs[0:NB, 2, P * k:P * (k + 1)], xs[0:NB, 2, P * k:P * (k + 1)], ps[0:NB, 2, :],
                                ALU.add).then_inc(n_done, 1)
            v.wait_ge(n_done, 112)
            v.wait_ge(s_gain, 32)
            for t in range(3):
                norm_rows(xs, gain, h2n, t, h2_ready)

            link(v.memset(lg, 0.0))
            v.wait_ge(t_log, 1)
            for t, r in enumerate(ROWS):
                ins = v.tensor_tensor(lg[0:r, t, :], bps[0:r, 64 * t:64 * t + G + NE], brt[0:r, :], ALU.add)
                link(ins)
            gl = lg[:, :, 0:G]

            def first_max(vals, w, idx, mx, hot, tmp):
                wide = [P, 3, w]
                ix = idx.unsqueeze(1).to_broadcast(wide)
                link(v.tensor_reduce(mx, vals, AX.X, ALU.max))
                link(v.tensor_tensor(tmp, vals, mx.unsqueeze(2).to_broadcast(wide), ALU.is_lt))
                link(v.tensor_scalar(tmp, tmp, 64.0, None, ALU.mult))
                link(v.tensor_tensor(tmp, tmp, ix, ALU.add))
                link(v.tensor_reduce(imin, tmp, AX.X, ALU.min))
                link(v.tensor_tensor(hot, imin.unsqueeze(2).to_broadcast(wide), ix, ALU.is_equal))

            first_max(gl, G, cc("gidx"), gmx, ghot, tw[:, :, 0:G])
            link(v.tensor_tensor(tex1[:, :, 0:G], gl, gmx.unsqueeze(2).to_broadcast([P, 3, G]), ALU.subtract))
            link(v.tensor_tensor(ew4, lg[:, :, G:G + NE].rearrange("p t (g e) -> p t g e", g=G),
                                 ghot.unsqueeze(3).to_broadcast([P, 3, G, EPG]), ALU.mult))
            link(v.tensor_reduce(el, ew4.rearrange("p t g e -> p t e g"), AX.X, ALU.add))
            first_max(el, EPG, cc("eidx"), m1, hot1, tw)
            link(v.tensor_scalar(tw, hot1, -BIG, None, ALU.mult))
            link(v.tensor_tensor(el2, el, tw, ALU.add))
            first_max(el2, EPG, cc("eidx"), m2, hot2, tw)
            link(v.tensor_tensor(tex1[:, :, G], m2, m1, ALU.subtract))
            v.sem_inc(t_lhs, 1)
            for hot, ohk in ((hot1, oh1), (hot2, oh2)):
                for t in range(3):
                    link(v.tensor_tensor(ohk[:, t, :].rearrange("p (g e) -> p g e", g=G),
                                         ghot[:, t, :].unsqueeze(2).to_broadcast([P, G, EPG]),
                                         hot[:, t, :].unsqueeze(1).to_broadcast([P, G, EPG]), ALU.mult))
            link(v.tensor_tensor(oh, oh1, oh2, ALU.add))
            v.sem_inc(t_oh, 1)
            v.wait_ge(t_e2, 1)
            link(v.tensor_reduce(gsum, tex1[:, :, 0:G], AX.X, ALU.add))
            link(v.reciprocal(gsum, gsum))
            link(v.tensor_scalar(wsum, tex1[:, :, G], 1.0, None, ALU.add))
            link(v.reciprocal(wsum, wsum))
            link(v.tensor_tensor(wk[:, :, 0], wsum, gsum, ALU.mult))
            link(v.tensor_tensor(wk[:, :, 1], wk[:, :, 0], tex1[:, :, G], ALU.mult))
            v.wait_ge(t_pos, 1)
            link(v.memset(xcnt, 0.0))
            for k in range(1, -(-T // CAP)):
                link(v.tensor_scalar(xtmp, mps[0:NE, 256:257], CAP * k + 0.5, None, ALU.is_gt))
                link(v.tensor_tensor(xcnt, xcnt, xtmp, ALU.add))
            link(v.tensor_copy(xcnt_b, xcnt.to_broadcast([NE, P])))
            v.sem_inc(t_x, 1)
            link(v.memset(posn, 0.0))
            for t, r in enumerate(ROWS):
                link(v.tensor_copy(posn[0:r, t, :], mps[0:r, NE * t:NE * (t + 1)]))
            v.wait_ge(t_tabs, 1)
            link(v.tensor_scalar(over, mps[:, 512:512 + NE], float(CAP), float(CAP * (NE - 1)), ALU.mult, ALU.add))
            link(v.tensor_tensor(over, over, cc("first"), ALU.subtract))
            for t in range(3):
                link(v.tensor_scalar(slotn[:, t, :], posn[:, t, :], CAP - 0.5, None, ALU.is_gt))
                link(v.tensor_tensor(slotn[:, t, :], slotn[:, t, :], over, ALU.mult))
                link(v.tensor_tensor(slotn[:, t, :], slotn[:, t, :], cc("first"), ALU.add))
                link(v.tensor_tensor(slotn[:, t, :], slotn[:, t, :], posn[:, t, :], ALU.add))
            for k, ohk in enumerate((oh1, oh2)):
                link(v.tensor_tensor(ohk, ohk, slotn, ALU.mult))
                link(v.tensor_reduce(addr[:, :, k], ohk, AX.X, ALU.add))
            link(v.tensor_copy(taddr_i[:, :], addr.rearrange("p t k -> p (t k)")))
            for q in range(6):
                a = addr.rearrange("p t k -> p (t k)")[:, q:q + 1]
                link(v.tensor_scalar(ge, cc("edge"), a, None, ALU.is_le))
                link(v.tensor_reduce(rem, ge[:, 1:NT + 1], AX.X, ALU.add))
                link(v.tensor_scalar(rem, rem, -float(CAP), a, ALU.mult, ALU.add))
                link(v.tensor_tensor(onB[:, q, :], ge[:, 0:NT], ge[:, 1:NT + 1], ALU.subtract))
                link(v.tensor_scalar(onB[:, q, :], onB[:, q, :], cc("tok")[:, q // 2:q // 2 + 1], None, ALU.mult))
                link(v.tensor_scalar(onA[:, q, :], cc("slot"), rem, None, ALU.is_equal))
            v.sem_inc(t_lhs, 1)
            link(v.tensor_copy(xcum, mps[0:1, 512:512 + NE]))
            for j in range(XT):
                if j == 0:
                    link(v.tensor_copy(xall, mps[0:1, 768:769]))
                link(v.tensor_scalar(xt2[:, 0:NE - 1], xcum[:, 1:NE], j + 0.5, None, ALU.is_lt))
                link(v.tensor_reduce(xexp[:, j:j + 1], xt2[:, 0:NE - 1], AX.X, ALU.add))
            link(v.tensor_copy(xexp[:, XT:XT + 1], xall))
            link(v.tensor_copy(texp_i[:, :], xexp))
            v.sem_inc(t_exp, 1)
            v.wait_ge(t_tabs, 2)
            link(v.tensor_copy(tidx_i[:, :], nps[0][0:CAP, 0:NT]))
            v.sem_inc(t_idx, 1)

            def hidden(par, n):
                v.wait_ge(e_sg, n)
                v.tensor_tensor(hid[par], hid[par], nps[par][0:CAP, DE:2 * DE], ALU.mult).then_inc(e_ac, 1)

            def y_copy(par, n, out_value):
                v.wait_ge(e_D, n)
                if out_value is not None:
                    v.wait_ge(y_out[par], out_value)
                v.tensor_copy(ysb[par], (bps, mps)[par][0:CAP, :]).then_inc(e_Dc, 1)

            hidden(0, 1)
            hidden(1, 2)
            y_copy(0, 1, None)
            hidden(0, 3)
            y_copy(1, 2, None)
            with v.Fori(0, (NE - 2) // 2) as i:
                for a in range(2):
                    if a == 0:
                        hidden(1, i * 2 + 4)
                        y_copy(0, i * 2 + 3, i * 16 + 16)
                    else:
                        with v.If(i < (NE - 2) // 2 - 1):
                            hidden(0, i * 2 + 5)
                        y_copy(1, i * 2 + 4, i * 16 + 16)
            extra = v.value_load(texp_i[0:1, XT:XT + 1], min_val=0, max_val=XT)
            with v.Fori(0, XT) as j:
                with v.If(extra > j):
                    hidden(0, j + (NE + 1))
                    y_copy(0, j + (NE + 1), j * 16 + 16 * (NE // 2))

            v.wait_ge(fgain, 16)
            for t, r in enumerate(ROWS):
                for k in range(2):
                    v.wait_ge(fg_in[k], 16 * (t + 1))
                    link(v.scalar_tensor_tensor(out=xs[0:r, t, :], in0=fbuf[k][0:r, :], scalar=wk[0:r, t, k:k + 1],
                                                in1=xs[0:r, t, :], op0=ALU.mult, op1=ALU.add))
                v.sem_inc(fy, 1)
                norm_rows(xs, gain, xs, t, o_x)


_IN = ["x_prompt", "x_sample", "cache_k", "cache_v", "state_ret", "page_table", "norm_mix", "w_in", "w_ret_o", "w_att_o",
       "w_o", "norm_ffn", "w_router_group", "b_router_group", "w_router_expert", "b_router_expert", "w_gate", "w_up",
       "w_down", "norm_final"]
_OUT = [(1, S, DM), (NB, 1, DM), (1, 1, S, AH, DH), (1, 1, S, AH, DH), (1, 1, RH, P, RDV), (1, NB, 1, AH, DH),
        (1, NB, 1, AH, DH), (1, NB, RH, P, RDV)]


def kernel(**inputs):
    import concourse.bacc as bacc
    from concourse.bass_utils import run_bass_kernel_spmd

    nc = bacc.Bacc("TRN2", target_bir_lowering=False, num_devices=1, dynamic_dma_scratch_size=8192)
    arrays, args = {}, []
    for name in _IN:
        a = np.ascontiguousarray(inputs[name])
        arrays["in_" + name] = a
        args.append(nc.dram_tensor("in_" + name, a.shape, mybir.dt.from_np(a.dtype), kind="ExternalInput").ap())
    arrays["shape_constants"] = shape_constants()
    args.append(nc.dram_tensor("shape_constants", [P, CW], F32, kind="ExternalInput").ap())
    for i, shape in enumerate(_OUT):
        args.append(nc.dram_tensor(f"out_{i}", list(shape), F32, kind="ExternalOutput").ap())
    build(nc, *args)
    r = run_bass_kernel_spmd(nc, [arrays], core_ids=[0])
    return tuple(r.results[0][f"out_{i}"] for i in range(len(_OUT)))
```
